# Optimizing a Trainium2 kernel written in Bass

```python
import math
import jax, jax.numpy as jnp
from jax import lax
import numpy as np

D_MODEL = 1024
BATCH = 1
SEQ = 256
DEPTH = 2

N_A_LAYERS = DEPTH // 2
N_B_LAYERS = DEPTH - N_A_LAYERS

N_HEADS = 8
Q_BLOCK = 128

DIFF_HEAD_DIM = 64
DIFF_V_DIM = 2 * DIFF_HEAD_DIM
DIFF_QK_WIDTH = N_HEADS * 2 * DIFF_HEAD_DIM
DIFF_V_WIDTH = N_HEADS * DIFF_V_DIM

NSA_HEAD_DIM = 128
NSA_KV_GROUPS = 2
NSA_HEADS_PER_GROUP = N_HEADS // NSA_KV_GROUPS
N_BRANCH = 3
CMP_LEN = 32
CMP_STRIDE = 16
CMP_HIDDEN = 256
SEL_BLOCK = 64
SEL_TOPN = 16
SEL_N_LOCAL = 2
WINDOW = 512
NSA_Q_BLOCK = 64
NSA_Q_WIDTH = N_HEADS * NSA_HEAD_DIM
NSA_GATE_WIDTH = N_HEADS * N_BRANCH
NSA_KV_WIDTH = N_BRANCH * 2 * NSA_KV_GROUPS * NSA_HEAD_DIM

REL_BUCKETS = 32
REL_MAX_DIST = 1024

PEER_HEADS = 8
PEER_N_KEYS = 128
PEER_N_EXPERTS = PEER_N_KEYS ** 2
PEER_QUERY_DIM = 256
PEER_TOPK = 16
PEER_TOKEN_BLOCK = 128

N_ADA = 6
NEG_INF = -1e30
FORCE = 1e9
EPS = 1e-6

kernel_name = 'yoco_diffattn_nsa_peer_hybrid'

def rms_norm(x, gain):
    xf = x.astype(jnp.float32)
    y = xf * lax.rsqrt(jnp.mean(xf * xf, axis=-1, keepdims=True) + EPS)
    return (y * gain.astype(jnp.float32)).astype(x.dtype)

def modulate(h, shift, scale):
    return h * (1 + scale[:, None, :]) + shift[:, None, :]

def rel_bucket(dist):
    max_exact = REL_BUCKETS // 2
    n = jnp.maximum(dist, 0)
    nf = jnp.maximum(n, 1).astype(jnp.float32)
    large = max_exact + (jnp.log(nf / max_exact) / math.log(REL_MAX_DIST / max_exact)
                         * (REL_BUCKETS - max_exact)).astype(jnp.int32)
    large = jnp.minimum(large, REL_BUCKETS - 1)
    return jnp.where(n < max_exact, n, large)

def masked_softmax(logits, mask):
    lf = jnp.where(mask, logits.astype(jnp.float32), NEG_INF)
    p = jax.nn.softmax(lf, axis=-1)
    return jnp.where(mask, p, 0.0)

def diff_attention(h, w_in, w_out, lam, q_gain, k_gain, subln_gain, rel_bias, layer_idx):
    B, S, _ = h.shape
    proj = h @ w_in
    q, k, v = jnp.split(proj, [DIFF_QK_WIDTH, 2 * DIFF_QK_WIDTH], axis=-1)
    q = rms_norm(q.reshape(B, S, N_HEADS, 2, DIFF_HEAD_DIM), q_gain)
    k = rms_norm(k.reshape(B, S, N_HEADS, 2, DIFF_HEAD_DIM), k_gain)
    v = v.reshape(B, S, N_HEADS, DIFF_V_DIM)
    lam_init = 0.8 - 0.6 * math.exp(-0.3 * layer_idx)
    lamf = lam.astype(jnp.float32)
    lam_full = jnp.exp(jnp.sum(lamf[0] * lamf[1])) - jnp.exp(jnp.sum(lamf[2] * lamf[3])) + lam_init
    nb = S // Q_BLOCK
    qb = q.reshape(B, nb, Q_BLOCK, N_HEADS, 2, DIFF_HEAD_DIM).transpose(1, 0, 2, 3, 4, 5)
    k_pos = jnp.arange(S)
    scale = DIFF_HEAD_DIM ** -0.5

    def block(args):
        qi, i = args
        q_pos = i * Q_BLOCK + jnp.arange(Q_BLOCK)
        dist = q_pos[:, None] - k_pos[None, :]
        mask = dist >= 0
        bias = rel_bias[rel_bucket(dist)].transpose(2, 0, 1)[None, :, None]
        logits = jnp.einsum('bthjd,bshjd->bhjts', qi, k) * scale + bias
        p = masked_softmax(logits, mask)
        attn = p[:, :, 0] - lam_full * p[:, :, 1]
        return jnp.einsum('bhts,bshe->bthe', attn.astype(v.dtype), v)

    o = lax.map(block, (qb, jnp.arange(nb)))
    o = o.transpose(1, 0, 2, 3, 4).reshape(B, S, N_HEADS, DIFF_V_DIM)
    o = rms_norm(o, subln_gain) * (1 - lam_init)
    return o.reshape(B, S, DIFF_V_WIDTH) @ w_out

def nsa_shared_kv(x, c_act, kv_norm, kv_ada_w, kv_ada_b, kv_w, cmp_pos, cmp_w1, cmp_b1, cmp_w2, k_gain):
    B, S, _ = x.shape
    G, HD = NSA_KV_GROUPS, NSA_HEAD_DIM
    shift, scale = jnp.split(c_act @ kv_ada_w + kv_ada_b, 2, axis=-1)
    h = modulate(rms_norm(x, kv_norm), shift, scale)
    kv = (h @ kv_w).reshape(B, S, N_BRANCH, 2, G, HD)
    kv = kv.transpose(2, 3, 0, 4, 1, 5)
    n_cmp = (S - CMP_LEN) // CMP_STRIDE + 1
    idx = np.arange(n_cmp)[:, None] * CMP_STRIDE + np.arange(CMP_LEN)[None, :]
    blocks = kv[0][:, :, :, idx]
    blocks = blocks + cmp_pos[:, None, None, None]
    flat = blocks.reshape(2, B, G, n_cmp, CMP_LEN * HD)
    hid = jax.nn.gelu(jnp.einsum('kbgnf,kfh->kbgnh', flat, cmp_w1) + cmp_b1[:, None, None, None])
    cmp = jnp.einsum('kbgnh,khd->kbgnd', hid, cmp_w2)
    k_cmp = rms_norm(cmp[0], k_gain[0])
    v_cmp = cmp[1]
    k_slc = rms_norm(kv[1, 0], k_gain[1])
    v_slc = kv[1, 1]
    k_win = rms_norm(kv[2, 0], k_gain[2])
    v_win = kv[2, 1]
    return (k_cmp, v_cmp, k_slc, v_slc, k_win, v_win)

def nsa_attention(h, w_in, b_gate, w_out, q_gain, rel_bias, k_cmp, v_cmp, k_slc, v_slc, k_win, v_win):
    B, S, _ = h.shape
    G, HG, HD, T = NSA_KV_GROUPS, NSA_HEADS_PER_GROUP, NSA_HEAD_DIM, NSA_Q_BLOCK
    proj = h @ w_in
    q = rms_norm(proj[..., :NSA_Q_WIDTH].reshape(B, S, G, HG, HD), q_gain)
    gates = jax.nn.sigmoid((proj[..., NSA_Q_WIDTH:] + b_gate).astype(jnp.float32))
    nb = S // T
    n_cmp = k_cmp.shape[2]
    n_sel = S // SEL_BLOCK
    top_n = min(SEL_TOPN, n_sel)
    cmp_start = np.arange(n_cmp) * CMP_STRIDE
    sel_start = np.arange(n_sel) * SEL_BLOCK
    overlap = np.clip(np.minimum(cmp_start[:, None] + CMP_LEN, sel_start[None, :] + SEL_BLOCK)
                      - np.maximum(cmp_start[:, None], sel_start[None, :]), 0, None) / CMP_LEN
    overlap = jnp.asarray(overlap, jnp.float32)
    cmp_end = jnp.asarray(cmp_start + CMP_LEN - 1, jnp.int32)
    k_blocks = k_slc.reshape(B, G, n_sel, SEL_BLOCK, HD)
    v_blocks = v_slc.reshape(B, G, n_sel, SEL_BLOCK, HD)
    pad = ((0, 0), (0, 0), (WINDOW, 0), (0, 0))
    k_win_p = jnp.pad(k_win, pad)
    v_win_p = jnp.pad(v_win, pad)
    tab = rel_bias.reshape(REL_BUCKETS, G, HG)
    qb = q.reshape(B, nb, T, G, HG, HD).transpose(1, 0, 3, 4, 2, 5)
    gb = gates.reshape(B, nb, T, G, HG, N_BRANCH).transpose(1, 0, 3, 4, 2, 5)
    scale = HD ** -0.5
    b_idx = jnp.arange(B)[:, None, None, None]
    g_idx = jnp.arange(G)[None, :, None, None]
    g_idx5 = jnp.arange(G)[None, :, None, None, None]
    blk = jnp.arange(n_sel)

    def block(args):
        qi, gi, i = args
        q_pos = i * T + jnp.arange(T)
        dist_c = q_pos[:, None] - cmp_end[None, :]
        mask_c = dist_c >= 0
        bias_c = tab[rel_bucket(dist_c)].transpose(2, 3, 0, 1)
        logit_c = jnp.einsum('bghtd,bgnd->bghtn', qi, k_cmp) * scale + bias_c
        p_c = masked_softmax(logit_c, mask_c)
        o_c = jnp.einsum('bghtn,bgnd->bghtd', p_c.astype(v_cmp.dtype), v_cmp)
        imp = jnp.einsum('bghtn,nj->bgtj', p_c, overlap)
        cur = q_pos // SEL_BLOCK
        back = cur[:, None] - blk[None, :]
        forced = (blk[None, :] == 0) | ((back >= 0) & (back < SEL_N_LOCAL))
        imp = jnp.where(forced, FORCE, imp)
        imp = jnp.where(back >= 0, imp, NEG_INF)
        top_score, sel = lax.top_k(imp, top_n)
        sel_valid = top_score >= 0
        ks = k_blocks[b_idx, g_idx, sel]
        vs = v_blocks[b_idx, g_idx, sel]
        key_pos = sel[..., None] * SEL_BLOCK + jnp.arange(SEL_BLOCK)
        dist_s = q_pos[:, None, None] - key_pos
        mask_s = ((dist_s >= 0) & sel_valid[..., None]).reshape(B, G, 1, T, top_n * SEL_BLOCK)
        bias_s = tab[rel_bucket(dist_s), g_idx5].transpose(0, 1, 5, 2, 3, 4)
        logit_s = jnp.einsum('bghtd,bgtnrd->bghtnr', qi, ks) * scale + bias_s
        p_s = masked_softmax(logit_s.reshape(B, G, HG, T, top_n * SEL_BLOCK), mask_s)
        o_s = jnp.einsum('bghtk,bgtkd->bghtd', p_s.astype(vs.dtype),
                         vs.reshape(B, G, T, top_n * SEL_BLOCK, HD))
        kw = lax.dynamic_slice_in_dim(k_win_p, i * T, WINDOW + T, axis=2)
        vw = lax.dynamic_slice_in_dim(v_win_p, i * T, WINDOW + T, axis=2)
        key_pos_w = i * T - WINDOW + jnp.arange(WINDOW + T)
        dist_w = q_pos[:, None] - key_pos_w[None, :]
        mask_w = (dist_w >= 0) & (dist_w < WINDOW) & (key_pos_w[None, :] >= 0)
        bias_w = tab[rel_bucket(dist_w)].transpose(2, 3, 0, 1)
        logit_w = jnp.einsum('bghtd,bgkd->bghtk', qi, kw) * scale + bias_w
        p_w = masked_softmax(logit_w, mask_w)
        o_w = jnp.einsum('bghtk,bgkd->bghtd', p_w.astype(vw.dtype), vw)
        gi = gi.astype(o_c.dtype)
        return (gi[..., 0:1] * o_c + gi[..., 1:2] * o_s + gi[..., 2:3] * o_w)

    o = lax.map(block, (qb, gb, jnp.arange(nb)))
    o = o.transpose(1, 0, 4, 2, 3, 5).reshape(B, S, NSA_Q_WIDTH)
    return o @ w_out

def peer_ffn(h, w_q, subkeys, u, v):
    B, S, D = h.shape
    T = PEER_TOKEN_BLOCK
    tokens = h.reshape((B * S) // T, T, D)
    half = PEER_QUERY_DIM // 2

    def block(xt):
        q = (xt @ w_q).reshape(T, PEER_HEADS, 2, half)
        s = jnp.einsum('thpd,pkd->thpk', q, subkeys).astype(jnp.float32)
        s1, i1 = lax.top_k(s[:, :, 0], PEER_TOPK)
        s2, i2 = lax.top_k(s[:, :, 1], PEER_TOPK)
        cand = (s1[..., :, None] + s2[..., None, :]).reshape(T, PEER_HEADS, PEER_TOPK * PEER_TOPK)
        cand_idx = (i1[..., :, None] * PEER_N_KEYS + i2[..., None, :]).reshape(T, PEER_HEADS, PEER_TOPK * PEER_TOPK)
        top_s, pos = lax.top_k(cand, PEER_TOPK)
        expert = jnp.take_along_axis(cand_idx, pos, axis=-1)
        gate = jax.nn.softmax(top_s, axis=-1)
        ue = u[expert]
        ve = v[expert]
        act = jax.nn.gelu(jnp.einsum('td,thkd->thk', xt, ue)).astype(jnp.float32)
        return jnp.einsum('thk,thkd->td', (gate * act).astype(ve.dtype), ve)

    return lax.map(block, tokens).reshape(B, S, D)

def setup_inputs(seed: int = 0) -> dict:
    key = jax.random.key(seed)
    ks = jax.random.split(key, 32)
    f32 = jnp.float32
    D = D_MODEL

    def nrm(k, shape, s):
        return jax.random.normal(k, shape, f32) * s

    def gain(k, shape):
        return 1.0 + 0.05 * jax.random.normal(k, shape, f32)

    return {
        'x': nrm(ks[0], (BATCH, SEQ, D), 1.0),
        'c': nrm(ks[1], (BATCH, D), 1.0),
        'rel_bias': nrm(ks[2], (REL_BUCKETS, N_HEADS), 0.5),
        'ada_w': nrm(ks[3], (DEPTH, D, N_ADA * D), 0.5 * D ** -0.5),
        'ada_b': nrm(ks[4], (DEPTH, N_ADA * D), 0.02),
        'norm_mix': gain(ks[5], (DEPTH, D)),
        'norm_ffn': gain(ks[6], (DEPTH, D)),
        'diff_w_in': nrm(ks[7], (N_A_LAYERS, D, 2 * DIFF_QK_WIDTH + DIFF_V_WIDTH), D ** -0.5),
        'diff_w_out': nrm(ks[8], (N_A_LAYERS, DIFF_V_WIDTH, D), DIFF_V_WIDTH ** -0.5),
        'diff_lambda': nrm(ks[9], (N_A_LAYERS, 4, DIFF_HEAD_DIM), 0.1),
        'diff_q_gain': gain(ks[10], (N_A_LAYERS, DIFF_HEAD_DIM)),
        'diff_k_gain': gain(ks[11], (N_A_LAYERS, DIFF_HEAD_DIM)),
        'diff_subln': gain(ks[12], (N_A_LAYERS, DIFF_V_DIM)),
        'kv_norm': gain(ks[13], (D,)),
        'kv_ada_w': nrm(ks[14], (D, 2 * D), 0.5 * D ** -0.5),
        'kv_ada_b': nrm(ks[15], (2 * D,), 0.02),
        'kv_w': nrm(ks[16], (D, NSA_KV_WIDTH), D ** -0.5),
        'cmp_pos': nrm(ks[17], (2, CMP_LEN, NSA_HEAD_DIM), 0.1),
        'cmp_w1': nrm(ks[18], (2, CMP_LEN * NSA_HEAD_DIM, CMP_HIDDEN), (CMP_LEN * NSA_HEAD_DIM) ** -0.5),
        'cmp_b1': nrm(ks[19], (2, CMP_HIDDEN), 0.02),
        'cmp_w2': nrm(ks[20], (2, CMP_HIDDEN, NSA_HEAD_DIM), CMP_HIDDEN ** -0.5),
        'nsa_k_gain': gain(ks[21], (N_BRANCH, NSA_HEAD_DIM)),
        'nsa_w_in': nrm(ks[22], (N_B_LAYERS, D, NSA_Q_WIDTH + NSA_GATE_WIDTH), D ** -0.5),
        'nsa_b_gate': nrm(ks[23], (N_B_LAYERS, NSA_GATE_WIDTH), 0.1),
        'nsa_w_out': nrm(ks[24], (N_B_LAYERS, NSA_Q_WIDTH, D), NSA_Q_WIDTH ** -0.5),
        'nsa_q_gain': gain(ks[25], (N_B_LAYERS, NSA_HEAD_DIM)),
        'peer_w_q': nrm(ks[26], (DEPTH, D, PEER_HEADS * PEER_QUERY_DIM), D ** -0.5),
        'peer_subkeys': nrm(ks[27], (DEPTH, 2, PEER_N_KEYS, PEER_QUERY_DIM // 2), (PEER_QUERY_DIM // 2) ** -0.5),
        'peer_u': nrm(ks[28], (DEPTH, PEER_N_EXPERTS, D), D ** -0.5),
        'peer_v': nrm(ks[29], (DEPTH, PEER_N_EXPERTS, D), 1.0),
    }

def reference(x, c, rel_bias, ada_w, ada_b, norm_mix, norm_ffn, diff_w_in, diff_w_out, diff_lambda,
              diff_q_gain, diff_k_gain, diff_subln, kv_norm, kv_ada_w, kv_ada_b, kv_w, cmp_pos, cmp_w1,
              cmp_b1, cmp_w2, nsa_k_gain, nsa_w_in, nsa_b_gate, nsa_w_out, nsa_q_gain, peer_w_q,
              peer_subkeys, peer_u, peer_v):
    c_act = jax.nn.silu(c)
    kv_shared = None
    for layer in range(DEPTH):
        if layer == N_A_LAYERS:
            kv_shared = nsa_shared_kv(x, c_act, kv_norm, kv_ada_w, kv_ada_b, kv_w, cmp_pos,
                                      cmp_w1, cmp_b1, cmp_w2, nsa_k_gain)
        sh_m, sc_m, g_m, sh_f, sc_f, g_f = jnp.split(c_act @ ada_w[layer] + ada_b[layer], N_ADA, axis=-1)
        h = modulate(rms_norm(x, norm_mix[layer]), sh_m, sc_m)
        if layer < N_A_LAYERS:
            y = diff_attention(h, diff_w_in[layer], diff_w_out[layer], diff_lambda[layer],
                               diff_q_gain[layer], diff_k_gain[layer], diff_subln[layer], rel_bias, layer)
        else:
            j = layer - N_A_LAYERS
            y = nsa_attention(h, nsa_w_in[j], nsa_b_gate[j], nsa_w_out[j], nsa_q_gain[j], rel_bias, *kv_shared)
        x = x + g_m[:, None, :] * y
        h = modulate(rms_norm(x, norm_ffn[layer]), sh_f, sc_f)
        x = x + g_f[:, None, :] * peer_ffn(h, peer_w_q[layer], peer_subkeys[layer], peer_u[layer], peer_v[layer])
    return x


_drawn_inputs = setup_inputs


def setup_inputs(seed=0):
    import zlib

    import numpy as np

    out = dict(_drawn_inputs(seed))
    spreads = {}
    factors = {'diff_lambda': 3.0,
     'kv_norm': 4.352,
     'kv_ada_b': 3.922,
     'cmp_pos': 3.056,
     'cmp_b1': 7.455,
     'nsa_k_gain': 5.681,
     'nsa_b_gate': 4.375,
     'nsa_q_gain': 6.229}
    for name, (base, spread) in spreads.items():
        noise = np.random.default_rng([zlib.crc32(name.encode()), seed]).standard_normal(out[name].shape)
        drawn = base * np.exp(spread * noise) if base else spread * noise
        out[name] = __import__('jax').numpy.asarray(drawn.astype(out[name].dtype))
    for name, factor in factors.items():
        out[name] = (out[name] * factor).astype(out[name].dtype)
    return out
```

```python
import math
from contextlib import ExitStack

import concourse.bass as bass
from concourse import mybir

ALU = mybir.AluOpType
ACT = mybir.ActivationFunctionType
AX = mybir.AxisListType
F32 = mybir.dt.float32
F32R = mybir.dt.float32r
U32 = mybir.dt.uint32

P = 128
D = 1024
T = 256
DC = D // P
TT = T // P
HEADS = 8
EPS = 1e-6
NEG = -1e30
LOWEST = -3e38
LAM_INIT = 0.8 - 0.6 * math.exp(-0.3 * 0)
N_CMP = 15
CMP_STRIDE = 16
CMP_LEN = 32
KEYS = 128
TOPK = 16
BUCKETS = 32
RAW_SLOTS = 4
SPLIT_SLOTS = 2
TOKENS_PER_TILE = 4
HALF = KEYS // 2

STREAM = [
    ("ada0_mix", 16, False), ("w_in", 24, True), ("ada0_gate", 8, False), ("w_out0", 8, True),
    ("ada0_ffn", 24, False), ("w_q0", 16, True), ("u0", 128, True), ("v0", 128, True),
    ("ada_kv", 16, False), ("ada1_mix", 24, False), ("kv_w", 12, True), ("cmp_w1", 16, False),
    ("nsa_q", 8, True), ("w_out1", 8, True),
    ("ada1_ffn", 24, False), ("w_q1", 16, True), ("u1", 128, True), ("v1", 128, True),
]
ADA_COL = {"ada0_mix": 0, "ada0_gate": 16, "ada0_ffn": 24, "ada_kv": 48, "ada1_mix": 64, "ada1_ffn": 88}


def plan():
    tile = split = whole = proj = 0
    out = {}
    for name, n, is_split in STREAM:
        out[name] = (tile, split, whole, proj, n, is_split)
        tile += n
        if is_split:
            split += n
            if name[0] != "v":
                proj += n
        else:
            whole += n
    return out


PLAN = plan()


class Arena:

    def __init__(self, tensor, at=0):
        self.tensor, self.at = tensor, at

    def take(self, *shape):
        n = 1
        for s in shape:
            n *= s
        view = self.tensor[:, self.at:self.at + n]
        self.at += n
        assert self.at <= self.tensor.shape[1]
        if len(shape) == 2:
            return view.rearrange("p (a b) -> p a b", a=shape[0])
        if len(shape) == 3:
            return view.rearrange("p (a b c) -> p a b c", a=shape[0], b=shape[1])
        return view


class Chain:

    def __init__(self, eng, sem):
        self.eng, self.sem, self.n = eng, sem, 0

    def step(self, ins):
        ins.then_inc(self.sem, 1)
        self.n += 1

    def sync(self):
        self.eng.wait_ge(self.sem, self.n)

    def done(self, ins):
        self.step(ins)
        self.sync()


def build(nc, a):
    with ExitStack() as ctx:
        def sb(name, shape, dt=F32):
            return ctx.enter_context(nc.sbuf_tensor(name, shape, dt))

        sems = {}

        def sem(name):
            if name not in sems:
                sems[name] = ctx.enter_context(nc.semaphore(name))
            return sems[name]

        x = sb("x_t", [P, DC, T])
        h_hi = sb("h_hi", [P, DC, T], F32R)
        h_lo = sb("h_lo", [P, DC, T], F32R)
        raw = sb("raw", [P, RAW_SLOTS, DC, P])
        w_hi = sb("w_hi", [P, SPLIT_SLOTS, DC, P], F32R)
        w_lo = sb("w_lo", [P, SPLIT_SLOTS, DC, P], F32R)
        arena = sb("arena", [P, T * KEYS])
        gates_mat = arena[:, :].rearrange("p (t k) -> p t k", t=T)
        bias_t = sb("bias_t", [P, HEADS, T])
        bias_c = sb("bias_c", [P, TT, HEADS, N_CMP])
        const = sb("const", [P, 4, P])
        ident, ones, halves, iota = (const[:, n, :] for n in range(4))
        mask_c = sb("mask_c", [P, TT, N_CMP])
        gains = sb("gains", [P, 5, DC])
        small = sb("small", [P, 16])
        mod_b = sb("mod_b", [P, 112])
        mods = sb("mods", [P, 112])
        c_act = sb("c_act", [P, 3, DC])
        lam = sb("lam", [P, 8])
        choice_t = sb("choice_t", [P, 3, T])
        onehots = sb("onehots", [P, TOKENS_PER_TILE, 2, P])
        act_ring = sb("act_ring", [P, 4, T])

        proj_ps = ctx.enter_context(nc.psum_tensor("proj_ps", [P, 2, 512], F32))
        misc_ps = ctx.enter_context(nc.psum_tensor("misc_ps", [P, 2, 512], F32))
        wide_ps = ctx.enter_context(nc.psum_tensor("wide_ps", [P, 4, 512], F32))
        mod_ps = misc_ps[:, 1, 0:112]

        act_dram = a["act_scratch"]

        base = Arena(arena)
        xr = base.take(DC, T)
        h = base.take(DC, T)
        sq = base.take(2, 1024)
        var = base.take(2, 1024)
        COMMON = base.at

        ph = Arena(arena, COMMON)
        qk = ph.take(16, T)
        v_t = ph.take(HEADS, T)
        v_rows = ph.take(TT, D)
        lg = ph.take(2, 2, 384)
        pr = ph.take(2, 2, 384)
        attn = ph.take(2, 384)
        attn_t = ph.take(2, 384)
        o_t = ph.take(HEADS, T)
        onehot_dist = ph.take(512)
        rel = ph.take(8)
        st = ph.take(2, 24)

        pn = Arena(arena, COMMON)
        kv_t = pn.take(12, T)
        q_t = pn.take(HEADS, T)
        v2 = pn.take(TT, 512)
        flat = pn.take(2, CMP_LEN * 30)
        hid = pn.take(2, 2, 30)
        cmp_k = pn.take(32)
        cmp_v = pn.take(2, P)
        w2 = pn.take(2, 2, P)
        pos_t = pn.take(2, CMP_LEN)
        w_gate = pn.take(DC, 24)
        b_gate = pn.take(24)
        gate = pn.take(TT, 24)
        lg1 = pn.take(2, 2, 384)
        pr1 = pn.take(2, 2, 384)
        pt1 = pn.take(2, 384)
        o1 = pn.take(HEADS, T)
        st1 = pn.take(2, 24)
        lc = pn.take(TT, HEADS * N_CMP)
        pc = pn.take(TT, HEADS * N_CMP)
        pct = pn.take(HEADS, T)
        stc = pn.take(4, 16)

        pf = Arena(arena, COMMON)
        query = pf.take(16, T)
        subkeys = pf.take(2, P)
        score = pf.take(16, T)
        pick2 = pf.take(256)
        cand = pf.take(256)
        cand2 = pf.take(256)
        best = pf.take(32)
        best_i = pf.take(32).bitcast(U32)
        best_f = pf.take(32)
        top_s = pf.take(16, TOPK)
        top_pos = pf.take(16).bitcast(U32)
        ab_u = pf.take(32).bitcast(U32)
        ab_f = pf.take(32)
        eq = pf.take(2, 256)
        chosen = pf.take(3, 256)
        gsum = pf.take(16)
        y_rows = Arena(arena).take(TT, D)

        q_gain0, k_gain0, subln = small[:, 0:1], small[:, 1:2], small[:, 2:3]
        nsa_kg = small[:, 3:6]
        nsa_qg = small[:, 6:7]
        b1 = small[:, 7:11]
        subln_s = small[:, 11:12]

        block = ctx.enter_context(nc.Block())

        loaded = [sem(f"tile_loaded{s}") for s in range(RAW_SLOTS)]
        rounded = sem("tile_rounded")
        split = sem("tile_split")
        used = sem("tile_used")
        whole_used = sem("whole_used")
        proj_free = [sem(f"proj_free{s}") for s in range(2)]

        def cols(v, lo, hi):
            return v[:, lo:hi, :].rearrange("p a b -> p (a b)")

        norm_blocks = {
            "qk": [(cols(qk, 4 * b, 4 * b + 4), 1024, halves, 64, [(0, 1024, q_gain0 if b < 2 else k_gain0)])
                   for b in range(4)],
            "subln": [(cols(o_t, 4 * b, 4 * b + 4), 1024, ones, P, [(0, 1024, subln_s)]) for b in range(2)],
            "keys": [(cols(kv_t, 4 * b, 4 * b + 2), 512, ones, P, [(0, 512, nsa_kg[:, b:b + 1])]) for b in (1, 2)],
            "cmp": [(cmp_k[:, 0:30], 30, ones, P, [(0, 30, nsa_kg[:, 0:1])])],
            "nsa_q": [(cols(q_t, 4 * b, 4 * b + 4), 1024, ones, P, [(0, 1024, nsa_qg)]) for b in range(2)],
        }
        norm_at, n = {}, 0
        for name, blocks in norm_blocks.items():
            norm_at[name] = n
            n += len(blocks)

        sq_ready, ss_ready, var_ready, std_ready, norm_done = (
            sem(s) for s in ("nb_square", "nb_sum", "nb_var", "nb_std", "nb_done"))
        x_updated = sem("x_updated")
        evacuated, n = {}, 0
        for name in ("w_in", "w_q0", "kv_w", "nsa_q", "w_q1"):
            n += PLAN[name][4] // 2
            evacuated[name] = n

        @block.sync
        def _(sp):
            def wait_slot(tile):
                prev = tile - RAW_SLOTS
                for name, (t0, s0, w0, _, n, is_split) in PLAN.items():
                    if t0 <= prev < t0 + n:
                        if is_split:
                            sp.wait_ge(split, s0 + prev - t0 + 1)
                        else:
                            sp.wait_ge(whole_used, w0 + prev - t0 + 1)

            def load(name, m):
                tile = PLAN[name][0] + m
                wait_slot(tile)
                sp.dma_start(raw[:, tile % RAW_SLOTS], a[name][m]).then_inc(loaded[tile % RAW_SLOTS], 16)

            sp.dma_start(x[:], a["x_t"]).then_inc(sem("x_loaded"), 16)
            for name, n, is_split in STREAM:
                t0, s0 = PLAN[name][:2]
                if n < 128:
                    for m in range(n):
                        load(name, m)
                    continue
                lay = name[1]
                for m in range(4):
                    load(name, m)
                    if name[0] == "v":
                        if m == 0:
                            for s in range(4):
                                sp.wait_ge(sem(f"act_stored{lay}_{s}"), 16 * (KEYS // 4))
                        sp.dma_start(act_ring[:, m], act_dram[m]).then_inc(sem(f"act_loaded{lay}_{m}"), 16)
                with sp.Fori(1, KEYS // 4) as i:
                    for c in range(4):
                        sp.wait_ge(split, s0 + 4 * i + c - 3)
                        sp.dma_start(raw[:, c], a[name][4 * i + c]).then_inc(loaded[c], 16)
                        if name[0] == "u":
                            sp.wait_ge(sem(f"act_gelu{lay}"), 4 * i + c - 3)
                            sp.dma_start(act_dram[4 * i + c - 4], act_ring[:, c]).then_inc(sem(f"act_stored{lay}_{c}"), 16)
                        else:
                            sp.wait_ge(sem(f"weighted{lay}"), 4 * i + c - 3)
                            sp.dma_start(act_ring[:, c], act_dram[4 * i + c]).then_inc(sem(f"act_loaded{lay}_{c}"), 16)
                if name[0] == "u":
                    for m in range(KEYS - 4, KEYS):
                        sp.wait_ge(sem(f"act_gelu{lay}"), m + 1)
                        sp.dma_start(act_dram[m], act_ring[:, m % 4]).then_inc(sem(f"act_stored{lay}_{m % 4}"), 16)
            for c in range(DC):
                sp.wait_ge(x_updated, 3 * DC + c + 1)
                sp.dma_start(a["out"][:, c], x[:, c]).then_inc(sem("out_stored"), 16)
            sp.wait_ge(sem("out_stored"), 16 * DC)

        FIRST = [(const, "const"), (c_act[:, 0], "c_t"), (mod_b, "mod_b"), (gains, "gains"),
                 (small[:, 0:11], "small"), (mask_c, "mask_c"), (lam[0:64, 0:4], "lam"),
                 (onehot_dist[0:BUCKETS + 1], "onehot_dist"), (rel[0:BUCKETS], "rel")]

        @block.gpsimd
        def _(pool):
            for dst, name in FIRST:
                pool.dma_start(dst[:] if dst in (const, mod_b, gains, mask_c) else dst, a[name]).then_inc(sem("params"), 16)
            nc.gpsimd.memset(rel[BUCKETS:BUCKETS + 1], NEG).then_inc(sem("rel_mask"), 1)
            for lay in range(2):
                pool.wait_ge(x_updated, DC * (2 * lay + 1))
                pool.dma_start(subkeys, a[f"subkeys{lay}"]).then_inc(sem("subkeys_loaded"), 16)
                if lay == 0:
                    pool.wait_ge(x_updated, 2 * DC)
                    for dst, name in ((w2, "w2"), (pos_t, "pos_t"), (w_gate, "w_gate"), (b_gate[0:1], "b_gate")):
                        pool.dma_start(dst, a[name]).then_inc(sem("nsa_params"), 16)

        @block.scalar
        def _(act):
            A = nc.scalar.activation

            def round_tile(name, m):
                t0, s0 = PLAN[name][:2]
                slot = (t0 + m) % RAW_SLOTS
                act.wait_ge(loaded[slot], 16 * ((t0 + m) // RAW_SLOTS + 1))
                if s0 + m >= SPLIT_SLOTS:
                    act.wait_ge(used, s0 + m - 1)
                A(w_hi[:, m % 2], raw[:, slot], ACT.Copy).then_inc(rounded, 1)

            def evac_proj(name, m, dst, func=ACT.Copy):
                t0, s0, _, p0 = PLAN[name][:4]
                act.wait_ge(used, s0 + m + 1)
                A(dst, proj_ps[:, m % 2, 0:T], func).then_inc(proj_free[m % 2], 1)

            def project(name, n, dst):
                for m in range(n + 1):
                    if m < n:
                        round_tile(name, m)
                    if m >= 1 and dst is not None:
                        evac_proj(name, m - 1, dst(m - 1))
                if dst is not None:
                    for b in range(2):
                        act.wait_ge(proj_free[b], evacuated[name])

            def layer_norm(k):
                if k == 0:
                    act.wait_ge(sem("x_loaded"), 16)
                else:
                    act.wait_ge(x_updated, DC * k)
                A(sq.rearrange("p a b -> p (a b)"), x[:].rearrange("p c t -> p (c t)"), ACT.Square).then_inc(sem("x_sq"), 1)
                act.wait_ge(sem("x_var"), k + 1)
                A(var[:, 0, 256:512], var[:, 0, 0:256], ACT.Sqrt).then_inc(sem("x_std"), 1)

            def modulate(k, scale_col, shift_col, free):
                act.wait_ge(sem("xr_ready"), k + 1)
                if free is not None:
                    act.wait_ge(used, free)
                for c in range(DC):
                    ins = A(h[:, c], xr[:, c], ACT.Identity, bias=mods[:, shift_col + c:shift_col + c + 1],
                            scale=mods[:, scale_col + c:scale_col + c + 1])
                    ins.then_inc(sem("h_ready"), 1)

            def round_h(k, src=None):
                act.wait_ge(sem("h_ready"), DC * (k + 1))
                A(h_hi[:], h if src is None else src, ACT.Copy).then_inc(sem("h_rounded"), 1)

            def norm_rows(name):
                blocks, b0 = norm_blocks[name], norm_at[name]
                for b in range(len(blocks) + 1):
                    if b < len(blocks):
                        view, w, _, _, _ = blocks[b]
                        if b0 + b >= 2:
                            act.wait_ge(ss_ready, b0 + b - 1)
                        A(sq[:, (b0 + b) % 2, 0:w], view, ACT.Square).then_inc(sq_ready, 1)
                    if b >= 1:
                        w = blocks[b - 1][1]
                        s = (b0 + b - 1) % 2
                        act.wait_ge(var_ready, b0 + b)
                        A(var[:, s, 0:w], var[:, s, 0:w], ACT.Sqrt).then_inc(std_ready, 1)

            act.wait_ge(sem("params"), 16 * len(FIRST))
            A(c_act[:, 1], c_act[:, 0], ACT.Exp, scale=-1.0).then_inc(sem("c_exp"), 1)
            act.wait_ge(sem("lam_sum"), 1)
            A(lam[:, 4:6], misc_ps[:, 0, 256:258], ACT.Exp).then_inc(sem("lam_exp"), 1)

            layer_norm(0)
            act.wait_ge(sem("mods"), 1)
            modulate(0, 8, 0, None)
            round_h(0)
            project("w_in", 24, lambda m: qk[:, m] if m < 16 else v_t[:, m - 16])
            norm_rows("qk")
            for b in range(4):
                act.wait_ge(sem("v_turned"), b + 1)
                A(v_rows[:, b // 2, 512 * (b % 2):512 * (b % 2) + 512], proj_ps[:, b % 2], ACT.Copy).then_inc(sem("v_rows"), 1)

            def exps(hd, probs, logits, stat, lay):
                act.wait_ge(sem(f"max{lay}"), hd + 1)
                if lay == 1 and hd >= 2:
                    act.wait_ge(sem("attn_turned1"), hd - 1)
                s = hd % 2
                for j in range(2):
                    for tt in range(2):
                        lo, hi = (256, 384) if tt == 0 else (0, 256)
                        A(probs[:, s, j, lo:hi], logits[:, s, j, lo:hi], ACT.Exp, bias=stat[:, s, 4 + 2 * tt + j:5 + 2 * tt + j],
                          accum_out=stat[:, s, 8 + 2 * tt + j:9 + 2 * tt + j]).then_inc(sem(f"exp{lay}"), 1)

            for hd in range(HEADS + 2):
                if hd < HEADS:
                    exps(hd, pr, lg, st, 0)
                if 1 <= hd <= HEADS:
                    k = hd - 1
                    act.wait_ge(sem("attn_turned0"), k + 1)
                    if k >= 2:
                        act.wait_ge(sem("pv0"), k - 1)
                    A(attn_t[:, k % 2], proj_ps[:, k % 2, 0:384], ACT.Copy).then_inc(sem("attn_t0"), 1)
                if hd >= 2:
                    k = hd - 2
                    act.wait_ge(sem("pv0"), k + 1)
                    A(o_t[:, k], misc_ps[:, k % 2, 256:512], ACT.Copy).then_inc(sem("o0"), 1)
            act.wait_ge(sem("o0"), HEADS)
            norm_rows("subln")
            act.wait_ge(norm_done, norm_at["subln"] + 2)
            A(h_hi[:], o_t, ACT.Copy).then_inc(sem("h_rounded"), 1)
            project("w_out0", 8, None)

            def peer(lay):
                k = 1 if lay == 0 else 3
                layer_norm(k)
                col = 24 if lay == 0 else 88
                act.wait_ge(sem("mods"), 3 if lay == 0 else 6)
                modulate(k, col + 8, col, None)
                act.wait_ge(sem("h_ready"), DC * (k + 1 + (lay == 1)))
                A(h_hi[:], h, ACT.Copy).then_inc(sem("h_rounded"), 1)
                project(f"w_q{lay}", 16, lambda m: query[:, m])
                for b in range(8):
                    act.wait_ge(sem(f"score_ps{lay}"), b + 1)
                    A(score[:, 2 * b:2 * b + 2, :].rearrange("p a b -> p (a b)"), wide_ps[:, b % 4], ACT.Copy)\
                        .then_inc(sem(f"score{lay}"), 1)

                name = f"u{lay}"
                t0, s0, _, p0 = PLAN[name][:4]

                def u_tile(i, c, first, build_gates):
                    act.wait_ge(loaded[c], 16 * (t0 // 4 + i + 1))
                    act.wait_ge(used, s0 + 4 * i + c - 1)
                    A(w_hi[:, c % 2], raw[:, c], ACT.Copy).then_inc(rounded, 1)
                    if first and c == 0:
                        return
                    u_finish(i, c, first)
                    if build_gates and not (first and c == 0):
                        gate_copy(i, c)

                def u_finish(i, c, first):
                    s = (c - 1) % 4
                    act.wait_ge(used, s0 + 4 * i + c)
                    if not first and not (c == 0 and isinstance(i, int) and i == 1):
                        act.wait_ge(sem(f"act_stored{lay}_{s}"), 16 * (i if c >= 1 else i - 1))
                    A(act_ring[:, s], proj_ps[:, s % 2, 0:T], ACT.Gelu_apprx_tanh)\
                        .then_inc(sem(f"act_gelu{lay}"), 1)

                def gate_copy(i, c):
                    m = 4 * i + c - 1 - HALF
                    act.wait_ge(sem(f"gates_ps{lay}"), m + 1)
                    A(arena[:, bass.ds(512 * m, 512)] if not isinstance(m, int) else arena[:, 512 * m:512 * m + 512],
                      wide_ps[:, (c - 1) % 2], ACT.Copy).then_inc(sem(f"gates_sb{lay}"), 1)

                for c in range(4):
                    u_tile(0, c, True, False)
                for c in range(4):
                    u_tile(1, c, False, False)
                with act.Fori(2, HALF // 4) as i:
                    for c in range(4):
                        u_tile(i, c, False, False)
                act.wait_ge(loaded[0], 16 * (t0 // 4 + HALF // 4 + 1))
                act.wait_ge(used, s0 + HALF - 1)
                A(w_hi[:, 0], raw[:, 0], ACT.Copy).then_inc(rounded, 1)
                u_finish(HALF // 4, 0, False)
                act.wait_ge(sem(f"top_shift{lay}"), 1)
                A(chosen[:, 2], top_s.rearrange("p a b -> p (a b)"), ACT.Exp).then_inc(sem(f"top_exp{lay}"), 1)
                for c in range(1, 4):
                    u_tile(HALF // 4, c, False, True)
                with act.Fori(HALF // 4 + 1, KEYS // 4) as i:
                    for c in range(4):
                        u_tile(i, c, False, True)
                u_finish(KEYS // 4, 0, False)
                gate_copy(KEYS // 4, 0)

                name = f"v{lay}"
                t0, s0 = PLAN[name][:2]

                def v_tile(i, c):
                    act.wait_ge(loaded[c], 16 * (t0 // 4 + i + 1))
                    act.wait_ge(used, s0 + 4 * i + c - 1)
                    A(w_hi[:, c % 2], raw[:, c], ACT.Copy).then_inc(rounded, 1)
                    act.wait_ge(sem(f"gated{lay}"), 4 * i + c + 1)
                    A(h_hi[:, c % 2], act_ring[:, c], ACT.Copy).then_inc(sem(f"act_rounded{lay}"), 1)

                act.wait_ge(used, s0)
                with act.Fori(0, KEYS // 4) as i:
                    for c in range(4):
                        v_tile(i, c)
                for b in range(4):
                    act.wait_ge(used, s0 + KEYS)
                    A(y_rows[:, b // 2, 512 * (b % 2):512 * (b % 2) + 512], wide_ps[:, b], ACT.Copy).then_inc(sem(f"y_rows{lay}"), 1)

            peer(0)

            layer_norm(2)
            act.wait_ge(sem("mods"), 4)
            modulate(2, 56, 48, None)
            round_h(2)
            project("kv_w", 12, lambda m: kv_t[:, m])
            act.wait_ge(sem("mods"), 5)
            modulate(2, 72, 64, PLAN["kv_w"][1] + 12)
            act.wait_ge(sem("h_ready"), DC * 4)
            A(h_hi[:], h, ACT.Copy).then_inc(sem("h_rounded"), 1)
            norm_rows("keys")
            for b in range(2):
                act.wait_ge(sem("v2_turned"), b + 1)
                A(v2[:, b], wide_ps[:, b], ACT.Copy).then_inc(sem("v2_rows"), 1)
            for k in range(2):
                act.wait_ge(whole_used, PLAN["cmp_w1"][2] + 8 * (k + 1))
                for half in range(2):
                    A(hid[:, k, half], (wide_ps[:, 2 + half] if k == 0 else proj_ps[:, half])[:, 0:30], ACT.Gelu_apprx_tanh,
                      bias=b1[:, 2 * k + half:2 * k + half + 1]).then_inc(sem("hid"), 1)
            act.wait_ge(sem("cmp_ps"), 1)
            A(cmp_k[:, 0:30], misc_ps[:, 0, 0:30], ACT.Copy).then_inc(sem("cmp_sb"), 1)
            for g in range(2):
                A(cmp_v[0:N_CMP, g], misc_ps[0:N_CMP, 0, 128 * (g + 1):128 * (g + 2)], ACT.Copy).then_inc(sem("cmp_sb"), 1)
            act.wait_ge(sem("cmp_sb"), 3)
            norm_rows("cmp")
            project("nsa_q", 8, lambda m: q_t[:, m])
            norm_rows("nsa_q")
            act.wait_ge(sem("gate_ps"), 1)
            A(gate.rearrange("p a b -> p (a b)"), misc_ps[:, 0, 0:48], ACT.Exp, scale=-1.0).then_inc(sem("gate_exp"), 1)
            act.wait_ge(sem("cmp_shift"), 1)
            A(pc.rearrange("p a b -> p (a b)"), lc.rearrange("p a b -> p (a b)"), ACT.Exp).then_inc(sem("cmp_exp"), 1)
            for b in range(4):
                act.wait_ge(sem("pct_ps"), b + 1)
                A(pct[0:N_CMP, 2 * b:2 * b + 2].rearrange("p a b -> p (a b)"), wide_ps[0:N_CMP, b], ACT.Copy).then_inc(sem("pct"), 1)
            for hd in range(HEADS + 2):
                if hd < HEADS:
                    exps(hd, pr1, lg1, st1, 1)
                if 1 <= hd <= HEADS:
                    k = hd - 1
                    act.wait_ge(sem("attn_turned1"), k + 1)
                    if k >= 1:
                        act.wait_ge(sem("pv1"), k)
                    for j in range(2):
                        A(pt1[:, j], proj_ps[:, j, 0:384], ACT.Copy).then_inc(sem("attn_t1"), 1)
                if hd >= 2:
                    k = hd - 2
                    act.wait_ge(sem("pv1"), k + 1)
                    A(o1[:, k], misc_ps[:, k % 2, 256:512], ACT.Copy).then_inc(sem("o1"), 1)
            act.wait_ge(sem("o1"), HEADS)
            A(h_hi[:], o1, ACT.Copy).then_inc(sem("h_rounded"), 1)
            project("w_out1", 8, None)
            peer(1)

        @block.vector
        def _(dve):
            V = nc.vector
            ch = Chain(dve, sem("dve_step"))

            def split_tile(name, m):
                t0, s0 = PLAN[name][:2]
                slot = (t0 + m) % RAW_SLOTS
                dve.wait_ge(rounded, s0 + m + 1)
                V.tensor_tensor(w_lo[:, m % 2], raw[:, slot], w_hi[:, m % 2].bitcast(F32), ALU.subtract).then_inc(split, 1)

            def split_h(k, src):
                dve.wait_ge(sem("h_rounded"), k + 1)
                V.tensor_tensor(h_lo[:], src, h_hi[:].bitcast(F32), ALU.subtract).then_inc(sem("h_split"), 1)

            def layer_norm(k):
                dve.wait_ge(sem("x_ss"), k + 1)
                V.tensor_scalar(var[:, 0, 0:256], misc_ps[:, 0, 0:256], 1.0 / D, EPS, ALU.mult, ALU.add).then_inc(sem("x_var"), 1)
                dve.wait_ge(sem("x_std"), k + 1)
                ch.done(V.reciprocal(var[:, 0, 512:768], var[:, 0, 256:512]))
                V.tensor_tensor(xr, x[:], var[:, 0, 512:768].unsqueeze(1).to_broadcast([P, DC, T]), ALU.mult).then_inc(sem("xr_ready"), 1)

            def modulation(k, name, n, gain_at):
                _, _, w0, _, cnt, _ = PLAN[name]
                col = ADA_COL[name]
                dve.wait_ge(whole_used, w0 + cnt)
                ins = V.tensor_tensor(mods[:, col:col + cnt], misc_ps[:, 1, col:col + cnt], mod_b[:, col:col + cnt], ALU.add)
                if gain_at is None:
                    ins.then_inc(sem("mods"), 1)
                    return
                ch.done(ins)
                sc = mods[:, col + 8:col + 16]
                V.scalar_tensor_tensor(sc, sc, 1.0, gains[:, gain_at], ALU.add, ALU.mult).then_inc(sem("mods"), 1)

            def norm_rows(name):
                blocks, b0 = norm_blocks[name], norm_at[name]
                for b, (view, w, _, feats, gs) in enumerate(blocks):
                    s = (b0 + b) % 2
                    dve.wait_ge(ss_ready, b0 + b + 1)
                    src = wide_ps[:, 2 * s:2 * s + 2].rearrange("p a b -> p (a b)")[:, 0:w]
                    V.tensor_scalar(var[:, s, 0:w], src, 1.0 / feats, EPS, ALU.mult, ALU.add).then_inc(var_ready, 1)
                    dve.wait_ge(std_ready, b0 + b + 1)
                    ch.done(V.reciprocal(var[:, s, 0:w], var[:, s, 0:w]))
                    (lo, hi, g), = gs
                    V.scalar_tensor_tensor(view, view, g, var[:, s, 0:w], ALU.mult, ALU.mult).then_inc(norm_done, 1)

            dve.wait_ge(sem("params"), 16 * len(FIRST))
            dve.wait_ge(sem("c_exp"), 1)
            ch.done(V.tensor_scalar(c_act[:, 1], c_act[:, 1], 1.0, None, ALU.add))
            ch.done(V.reciprocal(c_act[:, 1], c_act[:, 1]))
            V.tensor_tensor(c_act[:, 2], c_act[:, 0], c_act[:, 1], ALU.mult).then_inc(sem("c_ready"), 1)
            V.tensor_tensor(lam[0:64, 6:7], lam[0:64, 0:1], lam[0:64, 1:2], ALU.mult).then_inc(sem("lam_prod"), 1)
            V.tensor_tensor(lam[0:64, 7:8], lam[0:64, 2:3], lam[0:64, 3:4], ALU.mult).then_inc(sem("lam_prod"), 1)
            ch.step(V.tensor_scalar(subln_s, subln, 1.0 - LAM_INIT, None, ALU.mult))
            for b in range(4):
                dve.wait_ge(sem("bias_ps"), b + 1)
                V.tensor_copy(bias_t[:, :, 64 * b:64 * b + 64],
                              wide_ps[:, b].rearrange("p (w h) -> p h w", h=HEADS)).then_inc(sem("bias_sb"), 1)
            dve.wait_ge(sem("bias_ps"), 5)
            for tt in range(TT):
                V.tensor_copy(bias_c[:, tt], proj_ps[:, 0, 120 * tt:120 * tt + 120].rearrange("p (n h) -> p h n", h=HEADS))\
                    .then_inc(sem("bias_sb"), 1)
            dve.wait_ge(sem("lam_exp"), 1)
            ch.sync()
            ch.done(V.tensor_tensor(lam[:, 0:1], lam[:, 4:5], lam[:, 5:6], ALU.subtract))
            ch.done(V.tensor_scalar(lam[:, 1:2], lam[:, 0:1], LAM_INIT, -1.0, ALU.add, ALU.mult))

            layer_norm(0)
            modulation(0, "ada0_mix", 16, 0)
            split_h(0, h)
            for m in range(24):
                split_tile("w_in", m)
            norm_rows("qk")
            dve.wait_ge(sem("bias_sb"), 6)

            def softmax_front(hd, lay, logits, stat, scale):
                s = hd % 2
                dve.wait_ge(sem(f"logits{lay}"), hd + 1)
                if hd >= 2:
                    dve.wait_ge(sem(f"exp{lay}"), 4 * (hd - 1))
                ps = wide_ps[:, 2 * s:2 * s + 2]
                bias = bias_t[:, hd]
                ch.step(V.scalar_tensor_tensor(logits[:, s, :, 0:256], ps[:, :, 0:256], scale,
                                               bias.unsqueeze(1).to_broadcast([P, 2, 256]), ALU.mult, ALU.add))
                ch.step(V.scalar_tensor_tensor(logits[:, s, :, 256:384], ps[:, :, 256:384], scale,
                                                   bias[:, 128:256].unsqueeze(1).to_broadcast([P, 2, 128]), ALU.mult, ALU.add))
                ch.sync()
                ch.step(V.tensor_reduce(stat[:, s, 2:4], logits[:, s, :, 0:256], AX.X, ALU.max))
                ch.done(V.tensor_reduce(stat[:, s, 0:2], logits[:, s, :, 256:384], AX.X, ALU.max))
                V.tensor_scalar(stat[:, s, 4:8], stat[:, s, 0:4], -1.0, None, ALU.mult).then_inc(sem(f"max{lay}"), 1)

            def softmax_back0(hd):
                s = hd % 2
                dve.wait_ge(sem("exp0"), 4 * (hd + 1))
                if hd >= 2:
                    dve.wait_ge(sem("attn_turned0"), hd - 1)
                ch.done(V.reciprocal(st[:, s, 12:16], st[:, s, 8:12]))
                ch.done(V.tensor_scalar(st[:, s, 16:20], st[:, s, 12:16], lam[:, 1:2], None, ALU.mult))
                for tt, (lo, hi) in enumerate(((256, 384), (0, 256))):
                    ch.step(V.tensor_scalar(pr[:, s, 1, lo:hi], pr[:, s, 1, lo:hi], st[:, s, 17 + 2 * tt:18 + 2 * tt], None, ALU.mult))
                ch.sync()
                for tt, (lo, hi) in enumerate(((256, 384), (0, 256))):
                    V.scalar_tensor_tensor(attn[:, s, lo:hi], pr[:, s, 0, lo:hi], st[:, s, 12 + 2 * tt:13 + 2 * tt],
                                           pr[:, s, 1, lo:hi], ALU.mult, ALU.add).then_inc(sem("attn0"), 1)

            for hd in range(HEADS + 1):
                if hd < HEADS:
                    softmax_front(hd, 0, lg, st, 64 ** -0.5)
                if hd >= 1:
                    softmax_back0(hd - 1)
            norm_rows("subln")
            split_h(1, o_t)

            def out_project(name, gate_col, wait_mods):
                t0, s0 = PLAN[name][:2]
                dve.wait_ge(sem("mods"), wait_mods)
                for m in range(9):
                    if m < 8:
                        split_tile(name, m)
                    if m >= 1:
                        c = m - 1
                        dve.wait_ge(used, s0 + c + 1)
                        V.scalar_tensor_tensor(x[:, c], proj_ps[:, c % 2, 0:T], mods[:, gate_col + c:gate_col + c + 1], x[:, c],
                                               ALU.mult, ALU.add).then_inc(x_updated, 1)

            modulation(1, "ada0_gate", 8, None)
            out_project("w_out0", 16, 2)

            def peer(lay):
                k = 1 if lay == 0 else 3
                layer_norm(k)
                modulation(k, f"ada{lay}_ffn", 24, 1 if lay == 0 else 4)
                split_h(2 if lay == 0 else 6, h)
                for m in range(16):
                    split_tile(f"w_q{lay}", m)
                t0, s0 = PLAN[f"u{lay}"][:2]

                def u_split(i, c):
                    dve.wait_ge(rounded, s0 + 4 * i + c + 1)
                    V.tensor_tensor(w_lo[:, c % 2], raw[:, c], w_hi[:, c % 2].bitcast(F32), ALU.subtract).then_inc(split, 1)

                def top16(src, spare, vals, idx):
                    ch.sync()
                    ch.done(V.max(vals[:, 0:8], src))
                    ch.step(V.max_index(idx[:, 0:8], vals[:, 0:8], src))
                    ch.done(V.match_replace(spare, vals[:, 0:8], src, LOWEST))
                    ch.done(V.max(vals[:, 8:16], spare))
                    ch.step(V.max_index(idx[:, 8:16], vals[:, 8:16], spare))

                dve.wait_ge(sem(f"score{lay}"), 8)
                for i in range(HALF // 4):
                    u_split(i, 0)
                    top16(score[:, i, 0:128], pick2[:, 0:128], best[:, 0:16], best_i[:, 0:16])
                    u_split(i, 1)
                    top16(score[:, i, 128:256], pick2[:, 128:256], best[:, 16:32], best_i[:, 16:32])
                    ch.sync()
                    ch.step(V.tensor_copy(best_f, best_i))
                    ch.step(V.tensor_tensor(cand.rearrange("p (a b) -> p a b", a=16),
                                            best[:, 0:16].unsqueeze(2).to_broadcast([P, 16, 16]),
                                            best[:, 16:32].unsqueeze(1).to_broadcast([P, 16, 16]), ALU.add))
                    u_split(i, 2)
                    top16(cand, cand2, best[:, 0:16], top_pos)
                    ch.sync()
                    ch.step(V.tensor_copy(top_s[:, i], best[:, 0:16]))
                    u_split(i, 3)
                    ch.step(V.tensor_scalar(ab_u[:, 0:16], top_pos, 4, None, ALU.logical_shift_right))
                    ch.done(V.tensor_scalar(ab_u[:, 16:32], top_pos, 15, None, ALU.bitwise_and))
                    ch.done(V.tensor_copy(ab_f, ab_u))
                    eq4 = eq.rearrange("p r (k a) -> p r k a", k=16)
                    ch.done(V.tensor_tensor(eq4, ab_f.rearrange("p (r k) -> p r k", r=2).unsqueeze(3).to_broadcast([P, 2, 16, 16]),
                                            iota[:, 0:16].unsqueeze(1).unsqueeze(1).to_broadcast([P, 2, 16, 16]), ALU.is_equal))
                    ch.done(V.tensor_tensor(eq4, eq4, best_f.rearrange("p (r a) -> p r a", r=2).unsqueeze(2).to_broadcast([P, 2, 16, 16]),
                                            ALU.mult))
                    ch.done(V.tensor_reduce(chosen[:, 0:2, 16 * i:16 * i + 16], eq4, AX.X, ALU.add))
                ch.done(V.tensor_copy(gsum, top_s[:, :, 0:1].rearrange("p a b -> p (a b)")))
                V.tensor_tensor(top_s, top_s, gsum.unsqueeze(2).to_broadcast([P, 16, 16]), ALU.subtract).then_inc(sem(f"top_shift{lay}"), 1)
                dve.wait_ge(rounded, s0 + HALF + 1)
                V.tensor_tensor(w_lo[:, 0], raw[:, 0], w_hi[:, 0].bitcast(F32), ALU.subtract).then_inc(split, 1)
                dve.wait_ge(sem(f"top_exp{lay}"), 1)
                g3 = chosen[:, 2].rearrange("p (g k) -> p g k", g=16)
                ch.done(V.tensor_reduce(gsum, g3, AX.X, ALU.add))
                ch.done(V.reciprocal(gsum, gsum))
                V.tensor_tensor(g3, g3, gsum.unsqueeze(2).to_broadcast([P, 16, 16]), ALU.mult).then_inc(sem(f"chosen{lay}"), 1)
                dve.wait_ge(sem(f"choice_ps{lay}"), 1)
                ch.step(V.tensor_copy(choice_t[:, 0:2].rearrange("p a b -> p (a b)"), wide_ps[:, 2]))
                ch.done(V.tensor_copy(choice_t[:, 2], wide_ps[:, 3, 0:256]))

                def one_hot(m, c):
                    for q in range(TOKENS_PER_TILE):
                        if isinstance(m, int):
                            tok = TOKENS_PER_TILE * m + q
                            col = [choice_t[:, r, tok:tok + 1] for r in range(3)]
                        else:
                            col = [choice_t[:, r, bass.ds(TOKENS_PER_TILE * m + q, 1)] for r in range(3)]
                        if q == 0 and not (isinstance(m, int) and m == 0):
                            dve.wait_ge(sem(f"gates_ps{lay}"), m)
                        V.tensor_scalar(onehots[:, q, 0], iota, col[0], col[2], ALU.is_equal, ALU.mult).then_inc(sem(f"onehot{lay}"), 1)
                        V.tensor_scalar(onehots[:, q, 1], iota, col[1], None, ALU.is_equal).then_inc(sem(f"onehot{lay}"), 1)

                one_hot(0, 0)
                for c in range(1, 4):
                    u_split(HALF // 4, c)
                    one_hot(c, c)
                with dve.Fori(HALF // 4 + 1, KEYS // 4) as i:
                    for c in range(4):
                        u_split(i, c)
                        one_hot(4 * i + c - HALF, c)

                t0, s0 = PLAN[f"v{lay}"][:2]
                dve.wait_ge(sem(f"gates_sb{lay}"), HALF)
                with dve.Fori(0, KEYS // 4) as i:
                    for c in range(4):
                        dve.wait_ge(sem(f"act_loaded{lay}_{c}"), 16 * i + 16)
                        V.tensor_tensor(act_ring[:, c], act_ring[:, c],
                                        gates_mat[:, :, bass.ds(4 * i + c, 1)].rearrange("p t k -> p (t k)"), ALU.mult)\
                            .then_inc(sem(f"gated{lay}"), 1)
                        dve.wait_ge(rounded, s0 + 4 * i + c + 1)
                        V.tensor_tensor(w_lo[:, c % 2], raw[:, c], w_hi[:, c % 2].bitcast(F32), ALU.subtract).then_inc(split, 1)
                        dve.wait_ge(sem(f"act_rounded{lay}"), 4 * i + c + 1)
                        V.tensor_tensor(h_lo[:, c % 2], act_ring[:, c], h_hi[:, c % 2].bitcast(F32), ALU.subtract)\
                            .then_inc(sem(f"weighted{lay}"), 1)
                gcol = 40 if lay == 0 else 104
                for c in range(DC):
                    dve.wait_ge(sem(f"y_turned{lay}"), c + 1)
                    V.scalar_tensor_tensor(x[:, c], proj_ps[:, c % 2, 0:T], mods[:, gcol + c:gcol + c + 1], x[:, c],
                                           ALU.mult, ALU.add).then_inc(x_updated, 1)

            peer(0)

            layer_norm(2)
            modulation(2, "ada_kv", 16, 2)
            split_h(3, h)
            for m in range(12):
                split_tile("kv_w", m)
            modulation(3, "ada1_mix", 24, 3)
            split_h(4, h)
            for b in range(2):
                dve.wait_ge(proj_free[b], evacuated["kv_w"])
            dve.wait_ge(sem("nsa_params"), 64)
            for kind in range(2):
                for g in range(2):
                    src = kv_t[:, 2 * kind + g]
                    dst = flat[:, kind].rearrange("p (l m) -> p l m", m=30)
                    for part in range(2):
                        win = src[:, 16 * part:16 * part + 240].rearrange("p (n l) -> p l n", l=16)
                        V.tensor_tensor(dst[:, 16 * part:16 * part + 16, 15 * g:15 * g + 15], win,
                                        pos_t[:, kind, 16 * part:16 * part + 16].unsqueeze(2).to_broadcast([P, 16, 15]),
                                        ALU.add).then_inc(sem("flat"), 1)
            norm_rows("keys")
            norm_rows("cmp")
            for m in range(8):
                split_tile("nsa_q", m)
            norm_rows("nsa_q")
            dve.wait_ge(sem("gate_exp"), 1)
            gflat = gate.rearrange("p a b -> p (a b)")
            ch.done(V.tensor_scalar(gflat, gflat, 1.0, None, ALU.add))
            ch.done(V.reciprocal(gflat, gflat))
            dve.wait_ge(sem("cmp_logits"), 1)
            ch.done(V.scalar_tensor_tensor(lc.rearrange("p a b -> p (a b)"), misc_ps[:, 0, 48:288], 128 ** -0.5,
                                           bias_c[:].rearrange("p a h n -> p (a h n)"), ALU.mult, ALU.add))
            lc3 = lc.rearrange("p a (h n) -> p (a h) n", n=N_CMP)
            pc3 = pc.rearrange("p a (h n) -> p (a h) n", n=N_CMP)
            ch.done(V.tensor_reduce(stc[:, 0], lc3, AX.X, ALU.max))
            V.tensor_tensor(lc3, lc3, stc[:, 0].unsqueeze(2).to_broadcast([P, 16, N_CMP]), ALU.subtract).then_inc(sem("cmp_shift"), 1)
            dve.wait_ge(sem("cmp_exp"), 1)
            ch.done(V.tensor_reduce(stc[:, 1], pc3, AX.X, ALU.add))
            ch.done(V.reciprocal(stc[:, 2], stc[:, 1]))
            ch.done(V.tensor_tensor(stc[:, 3].rearrange("p (a h) -> p a h", a=2), stc[:, 2].rearrange("p (a h) -> p a h", a=2),
                                    gate.rearrange("p a (h r) -> p a h r", r=3)[:, :, :, 0], ALU.mult))
            ch.done(V.tensor_tensor(pc3, pc3, stc[:, 3].unsqueeze(2).to_broadcast([P, 16, N_CMP]), ALU.mult))
            for tt in range(TT):
                V.tensor_tensor(pc[:, tt].rearrange("p (h n) -> p h n", n=N_CMP), pc[:, tt].rearrange("p (h n) -> p h n", n=N_CMP),
                                mask_c[:, tt].unsqueeze(1).to_broadcast([P, HEADS, N_CMP]), ALU.mult).then_inc(sem("pc"), 1)

            def softmax_back1(hd):
                s = hd % 2
                dve.wait_ge(sem("exp1"), 4 * (hd + 1))
                ch.done(V.reciprocal(st1[:, s, 12:16], st1[:, s, 8:12]))
                ch.done(V.tensor_tensor(st1[:, s, 16:20].rearrange("p (a b) -> p a b", a=2), st1[:, s, 12:16].rearrange("p (a b) -> p a b", a=2),
                                        gate[:, :, 3 * hd + 1:3 * hd + 3], ALU.mult))
                for tt, (lo, hi) in enumerate(((256, 384), (0, 256))):
                    for j in range(2):
                        V.tensor_scalar(pr1[:, s, j, lo:hi], pr1[:, s, j, lo:hi], st1[:, s, 16 + 2 * tt + j:17 + 2 * tt + j], None,
                                        ALU.mult).then_inc(sem("attn1"), 1)

            for hd in range(HEADS + 1):
                if hd < HEADS:
                    softmax_front(hd, 1, lg1, st1, 128 ** -0.5)
                if hd >= 1:
                    softmax_back1(hd - 1)
            split_h(5, o1)
            out_project("w_out1", 80, 5)
            peer(1)

        @block.tensor
        def _(pe):
            M = nc.tensor.matmul

            def ada(name):
                t0, _, w0, _, n, _ = PLAN[name]
                before = list(ADA_COL).index(name)
                if before:
                    pe.wait_ge(sem("mods"), before)
                for m in range(n):
                    slot = (t0 + m) % RAW_SLOTS
                    pe.wait_ge(loaded[slot], 16 * ((t0 + m) // RAW_SLOTS + 1))
                    col = ADA_COL[name] + m
                    for c in range(DC):
                        mm = M(misc_ps[:, 1, col:col + 1], raw[:, slot, c], c_act[:, 2, c:c + 1], start=(c == 0), stop=(c == DC - 1))
                    mm.then_inc(whole_used, 1)

            def split_product(out, slot):
                for c in range(DC):
                    M(out, w_hi[:, slot, c], h_hi[:, c], start=(c == 0), stop=False)
                    M(out, w_hi[:, slot, c], h_lo[:, c], start=False, stop=False)
                    mm = M(out, w_lo[:, slot, c], h_hi[:, c], start=False, stop=(c == DC - 1))
                return mm

            freed = [0, 0]

            def project(name, n, signalled=True):
                s0 = PLAN[name][1]
                for m in range(n):
                    pe.wait_ge(split, s0 + m + 1)
                    if signalled:
                        if m >= 2:
                            pe.wait_ge(proj_free[m % 2], freed[m % 2])
                        freed[m % 2] += 1
                    elif m >= 2:
                        pe.wait_ge(x_updated, (0 if name == "w_out0" else 2 * DC) + m - 1)
                    split_product(proj_ps[:, m % 2, 0:T], m % 2).then_inc(used, 1)
                if signalled:
                    for s in range(2):
                        pe.wait_ge(proj_free[s], freed[s])

            def layer_norm(k):
                pe.wait_ge(sem("x_sq"), k + 1)
                s = sq.rearrange("p a (c t) -> p (a c) t", t=T)
                for c in range(DC):
                    mm = M(misc_ps[:, 0, 0:256], ones, s[:, c], start=(c == 0), stop=(c == DC - 1))
                mm.then_inc(sem("x_ss"), 1)

            def norm_rows(name):
                blocks, b0 = norm_blocks[name], norm_at[name]
                for b, (view, w, mat, _, _) in enumerate(blocks):
                    s = (b0 + b) % 2
                    pe.wait_ge(sq_ready, b0 + b + 1)
                    if b0 + b >= 2:
                        pe.wait_ge(var_ready, b0 + b - 1)
                    for piece in range(0, w, 512):
                        e = min(512, w - piece)
                        mm = M(wide_ps[:, 2 * s + piece // 512, 0:e], mat, sq[:, s, piece:piece + e], start=True, stop=True)
                    mm.then_inc(ss_ready, 1)

            pe.wait_ge(sem("params"), 16 * len(FIRST))
            pe.wait_ge(sem("rel_mask"), 1)
            pe.wait_ge(sem("lam_prod"), 2)
            M(misc_ps[:, 0, 256:258], ones[0:64, :], lam[0:64, 6:8], start=True, stop=True).then_inc(sem("lam_sum"), 1)
            K = BUCKETS + 1
            for w in range(T):
                mm = M(wide_ps[:, w // 64, 8 * (w % 64):8 * (w % 64) + 8], onehot_dist[0:K, 383 - w:511 - w], rel[0:K, :],
                       start=True, stop=True)
                if w % 64 == 63:
                    mm.then_inc(sem("bias_ps"), 1)
            for tt in range(TT):
                for n in range(N_CMP):
                    at = 224 + P * tt - CMP_STRIDE * n
                    col = 8 * (N_CMP * tt + n)
                    mm = M(proj_ps[:, 0, col:col + 8], onehot_dist[0:K, at:at + P], rel[0:K, :], start=True, stop=True)
            mm.then_inc(sem("bias_ps"), 1)
            pe.wait_ge(sem("c_ready"), 1)
            pe.wait_ge(sem("lam_exp"), 1)
            layer_norm(0)
            ada("ada0_mix")
            pe.wait_ge(sem("h_split"), 1)
            pe.wait_ge(sem("bias_sb"), 6)
            project("w_in", 24)
            norm_rows("qk")
            for b in range(4):
                if b >= 2:
                    pe.wait_ge(sem("v_rows"), b - 1)
                for q in range(4):
                    mm = nc.tensor.transpose(proj_ps[:, b % 2, 128 * q:128 * q + 128],
                                             v_t[:, 4 * (b % 2) + q, 128 * (b // 2):128 * (b // 2) + 128], ident)
                mm.then_inc(sem("v_turned"), 1)

            def logits0(hd):
                s = 2 * (hd % 2)
                if hd >= 2:
                    pe.wait_ge(sem("max0"), hd - 1)
                for j in range(2):
                    r = slice(64 * j, 64 * j + 64)
                    q, k = qk[r, hd], qk[r, 8 + hd]
                    M(wide_ps[:, s + j, 0:256], q[:, 128:256], k, start=True, stop=True)
                    mm = M(wide_ps[:, s + j, 256:384], q[:, 0:128], k[:, 0:128], start=True, stop=True)
                mm.then_inc(sem("logits0"), 1)

            def turn0(hd):
                s = hd % 2
                pe.wait_ge(sem("attn0"), 2 * hd + 2)
                if hd >= 2:
                    pe.wait_ge(sem("attn_t0"), hd - 1)
                for n, at in enumerate((256, 0, 128)):
                    mm = nc.tensor.transpose(proj_ps[:, s, 128 * n:128 * n + 128], attn[:, s, at:at + 128], ident)
                mm.then_inc(sem("attn_turned0"), 1)

            def pv0(hd):
                s = hd % 2
                pe.wait_ge(sem("attn_t0"), hd + 1)
                if hd >= 2:
                    pe.wait_ge(sem("o0"), hd - 1)
                M(misc_ps[:, s, 256:512], v_rows[:, 0, 128 * hd:128 * hd + 128], attn_t[:, s, 0:256], start=True, stop=False)
                M(misc_ps[:, s, 384:512], v_rows[:, 1, 128 * hd:128 * hd + 128], attn_t[:, s, 256:384],
                  start=False, stop=True).then_inc(sem("pv0"), 1)

            pe.wait_ge(norm_done, 4)
            pe.wait_ge(sem("v_rows"), 4)
            for hd in range(HEADS + 2):
                if hd < HEADS:
                    logits0(hd)
                if 1 <= hd <= HEADS:
                    turn0(hd - 1)
                if hd >= 2:
                    pv0(hd - 2)
            pe.wait_ge(sem("o0"), HEADS)
            ada("ada0_gate")
            norm_rows("subln")
            pe.wait_ge(sem("h_split"), 2)
            project("w_out0", 8, signalled=False)

            def peer(lay):
                k = 1 if lay == 0 else 3
                layer_norm(k)
                ada(f"ada{lay}_ffn")
                pe.wait_ge(sem("h_split"), 3 if lay == 0 else 7)
                project(f"w_q{lay}", 16)
                pe.wait_ge(sem("subkeys_loaded"), 16 * (lay + 1))
                for b in range(8):
                    if b >= 4:
                        pe.wait_ge(sem(f"score{lay}"), b - 3)
                    for q in range(4):
                        n = 4 * (b % 4) + q
                        mm = M(wide_ps[:, b % 4, 128 * q:128 * q + 128], query[:, n, 128 * (b // 4):128 * (b // 4) + 128],
                               subkeys[:, n % 2], start=True, stop=True)
                    mm.then_inc(sem(f"score_ps{lay}"), 1)
                s0 = PLAN[f"u{lay}"][1]

                def u_tile(i, c, first):
                    pe.wait_ge(split, s0 + 4 * i + c + 1)
                    if not (first and c < 2):
                        pe.wait_ge(sem(f"act_gelu{lay}"), 4 * i + c - 1)
                    split_product(proj_ps[:, c % 2, 0:T], c % 2).then_inc(used, 1)

                def gates(m, c, first):
                    pe.wait_ge(sem(f"onehot{lay}"), 2 * TOKENS_PER_TILE * (m + 1))
                    if not first:
                        pe.wait_ge(sem(f"gates_sb{lay}"), m - 1)
                    for q in range(TOKENS_PER_TILE):
                        mm = M(wide_ps[:, c % 2, 128 * q:128 * q + 128], onehots[:, q, 0], onehots[:, q, 1], start=True, stop=True)
                    mm.then_inc(sem(f"gates_ps{lay}"), 1)

                for c in range(4):
                    u_tile(0, c, True)
                with pe.Fori(1, HALF // 4) as i:
                    for c in range(4):
                        u_tile(i, c, False)
                u_tile(HALF // 4, 0, False)
                pe.wait_ge(sem(f"chosen{lay}"), 1)
                for r in range(3):
                    for tt in range(TT):
                        at = 256 * r + 128 * tt
                        mm = nc.tensor.transpose(wide_ps[:, 2 + at // 512, at % 512:at % 512 + 128],
                                                 chosen[:, r, 128 * tt:128 * tt + 128], ident)
                mm.then_inc(sem(f"choice_ps{lay}"), 1)
                gates(0, 0, True)
                for c in range(1, 4):
                    u_tile(HALF // 4, c, False)
                    gates(c, c, c < 2)
                with pe.Fori(HALF // 4 + 1, KEYS // 4) as i:
                    for c in range(4):
                        u_tile(i, c, False)
                        gates(4 * i + c - HALF, c, False)

                s0 = PLAN[f"v{lay}"][1]

                def v_tile(i, c, first, last):
                    pe.wait_ge(split, s0 + 4 * i + c + 1)
                    pe.wait_ge(sem(f"weighted{lay}"), 4 * i + c + 1)
                    s = c % 2
                    for tt in range(TT):
                        tok = slice(128 * tt, 128 * tt + 128)
                        for half in range(2):
                            out = wide_ps[:, 2 * tt + half]
                            vh = w_hi[:, s, 4 * half:4 * half + 4].rearrange("p a b -> p (a b)")
                            vl = w_lo[:, s, 4 * half:4 * half + 4].rearrange("p a b -> p (a b)")
                            M(out, h_hi[:, s, tok], vh, start=first, stop=False)
                            M(out, h_hi[:, s, tok], vl, start=False, stop=False)
                            mm = M(out, h_lo[:, s, tok], vh, start=False, stop=last)
                    mm.then_inc(used, 1)

                pe.wait_ge(sem(f"gates_sb{lay}"), HALF)
                for c in range(4):
                    v_tile(0, c, c == 0, False)
                with pe.Fori(1, KEYS // 4 - 1) as i:
                    for c in range(4):
                        v_tile(i, c, False, False)
                for c in range(4):
                    v_tile(KEYS // 4 - 1, c, False, c == 3)
                pe.wait_ge(sem(f"act_gelu{lay}"), KEYS)
                for c in range(DC):
                    pe.wait_ge(sem(f"y_rows{lay}"), 4)
                    if c >= 2:
                        pe.wait_ge(x_updated, DC * (2 * lay + 1) + c - 1)
                    for tt in range(TT):
                        mm = nc.tensor.transpose(proj_ps[:, c % 2, 128 * tt:128 * tt + 128],
                                                 y_rows[:, tt, 128 * c:128 * c + 128], ident)
                    mm.then_inc(sem(f"y_turned{lay}"), 1)

            peer(0)

            layer_norm(2)
            ada("ada_kv")
            ada("ada1_mix")
            pe.wait_ge(sem("h_split"), 4)
            project("kv_w", 12)
            norm_rows("keys")
            pe.wait_ge(var_ready, norm_at["keys"] + 2)
            for b in range(2):
                for q in range(4):
                    src = kv_t[:, 4 * (1 + q // 2) + 2 + q % 2, 128 * b:128 * b + 128]
                    mm = nc.tensor.transpose(wide_ps[:, b, 128 * q:128 * q + 128], src, ident)
                mm.then_inc(sem("v2_turned"), 1)
            pe.wait_ge(sem("flat"), 8)
            t0, _, w0, _, _, _ = PLAN["cmp_w1"]
            for k in range(2):
                for m in range(8):
                    tile = t0 + 8 * k + m
                    pe.wait_ge(loaded[tile % 4], 16 * (tile // 4 + 1))
                    for q in range(4):
                        pos = 4 * m + q
                        for half in range(2):
                            mm = M((wide_ps[:, 2 + half] if k == 0 else proj_ps[:, half])[:, 0:30], raw[:, tile % 4, 2 * q + half],
                                   flat[:, k, 30 * pos:30 * pos + 30], start=(pos == 0), stop=(pos == 31))
                    mm.then_inc(whole_used, 1)
            pe.wait_ge(sem("hid"), 4)
            for half in range(2):
                M(misc_ps[:, 0, 0:30], w2[:, 0, half], hid[:, 0, half], start=(half == 0), stop=(half == 1))
            for g in range(2):
                for half in range(2):
                    mm = M(misc_ps[0:N_CMP, 0, 128 * (g + 1):128 * (g + 2)], hid[:, 1, half, 15 * g:15 * g + 15], w2[:, 1, half],
                           start=(half == 0), stop=(half == 1))
            mm.then_inc(sem("cmp_ps"), 1)
            pe.wait_ge(sem("cmp_sb"), 3)
            pe.wait_ge(sem("v2_rows"), 2)
            norm_rows("cmp")
            pe.wait_ge(sem("h_split"), 5)
            project("nsa_q", 8)
            for tt in range(TT):
                for c in range(DC):
                    M(misc_ps[:, 0, 24 * tt:24 * tt + 24], h[:, c, 128 * tt:128 * tt + 128], w_gate[:, c], start=(c == 0), stop=False)
                mm = M(misc_ps[:, 0, 24 * tt:24 * tt + 24], ones[0:1, :], b_gate[0:1, :], start=False, stop=True)
            mm.then_inc(sem("gate_ps"), 1)
            norm_rows("nsa_q")
            pe.wait_ge(norm_done, norm_at["nsa_q"] + 2)
            pe.wait_ge(sem("gate_exp"), 1)
            for tt in range(TT):
                for hd in range(HEADS):
                    col = 48 + 15 * (8 * tt + hd)
                    g = hd // 4
                    mm = M(misc_ps[:, 0, col:col + 15], q_t[:, hd, 128 * tt:128 * tt + 128], cmp_k[:, 15 * g:15 * g + 15],
                           start=True, stop=True)
            mm.then_inc(sem("cmp_logits"), 1)
            pe.wait_ge(sem("pc"), 2)
            for hd in range(HEADS):
                for tt in range(TT):
                    at = 256 * (hd % 2) + 128 * tt
                    mm = nc.tensor.transpose(wide_ps[0:N_CMP, hd // 2, at:at + 128], pc[:, tt, 15 * hd:15 * hd + 15], ident)
                if hd % 2:
                    mm.then_inc(sem("pct_ps"), 1)
            pe.wait_ge(sem("pct"), 4)

            def logits1(hd):
                s = 2 * (hd % 2)
                if hd >= 2:
                    pe.wait_ge(sem("max1"), hd - 1)
                for j in range(2):
                    q, k = q_t[:, hd], kv_t[:, 4 * (1 + j) + hd // 4]
                    M(wide_ps[:, s + j, 0:256], q[:, 128:256], k, start=True, stop=True)
                    mm = M(wide_ps[:, s + j, 256:384], q[:, 0:128], k[:, 0:128], start=True, stop=True)
                mm.then_inc(sem("logits1"), 1)

            def turn1(hd):
                s = hd % 2
                pe.wait_ge(sem("attn1"), 4 * hd + 4)
                if hd >= 1:
                    pe.wait_ge(sem("attn_t1"), 2 * hd)
                for j in range(2):
                    for n, at in enumerate((256, 0, 128)):
                        mm = nc.tensor.transpose(proj_ps[:, j, 128 * n:128 * n + 128], pr1[:, s, j, at:at + 128], ident)
                mm.then_inc(sem("attn_turned1"), 1)

            def pv1(hd):
                pe.wait_ge(sem("attn_t1"), 2 * hd + 2)
                if hd >= 2:
                    pe.wait_ge(sem("o1"), hd - 1)
                s, g = hd % 2, hd // 4
                M(misc_ps[:, s, 256:512], cmp_v[0:N_CMP, g], pct[0:N_CMP, hd], start=True, stop=False)
                for j in range(2):
                    col = 128 * (2 * j + g)
                    M(misc_ps[:, s, 256:512], v2[:, 0, col:col + 128], pt1[:, j, 0:256], start=False, stop=False)
                    mm = M(misc_ps[:, s, 384:512], v2[:, 1, col:col + 128], pt1[:, j, 256:384], start=False, stop=(j == 1))
                mm.then_inc(sem("pv1"), 1)

            for hd in range(HEADS + 2):
                if hd < HEADS:
                    logits1(hd)
                if 1 <= hd <= HEADS:
                    turn1(hd - 1)
                if hd >= 2:
                    pv1(hd - 2)
            pe.wait_ge(sem("h_split"), 6)
            project("w_out1", 8, signalled=False)
            peer(1)


def distance_buckets():
    import numpy as np
    dist = np.arange(-255, 257)
    n = np.maximum(dist, 0)
    exact = BUCKETS // 2
    nf = np.maximum(n, 1).astype(np.float32)
    large = exact + (np.log(nf / np.float32(exact)) / np.float32(math.log(1024 / exact)) * np.float32(BUCKETS - exact)).astype(np.int32)
    bucket = np.where(n < exact, n, np.minimum(large, BUCKETS - 1))
    bucket[dist < 0] = BUCKETS
    return (np.arange(BUCKETS + 1)[:, None] == bucket[None]).astype(np.float32)


def kernel(**inputs):
    import numpy as np
    import concourse.bacc as bacc
    from concourse.bass_utils import run_bass_kernel_spmd

    i = {k: np.asarray(v) for k, v in inputs.items()}
    C = np.ascontiguousarray

    def tiles(w):
        return C(w.reshape(DC, P, -1, P).transpose(2, 1, 0, 3))

    def columns(*vectors):
        return C(np.concatenate([v.reshape(-1, P) for v in vectors]).T)

    ada = [tiles(i["ada_w"][l]) for l in range(2)]
    w_in = tiles(i["diff_w_in"][0])
    arrays = {
        "x_t": C(i["x"][0].T.reshape(DC, P, T).transpose(1, 0, 2)),
        "c_t": columns(i["c"][0]),
        "ada0_mix": ada[0][0:16], "ada0_gate": ada[0][16:24], "ada0_ffn": ada[0][24:48],
        "ada_kv": tiles(i["kv_ada_w"]), "ada1_mix": ada[1][0:24], "ada1_ffn": ada[1][24:48],
        "w_in": w_in, "w_out0": tiles(i["diff_w_out"][0]), "kv_w": tiles(i["kv_w"]),
        "cmp_w1": C(i["cmp_w1"].reshape(2, 8, 4, P, 256).transpose(0, 1, 3, 2, 4)).reshape(16, P, DC, P),
        "nsa_q": tiles(i["nsa_w_in"][0][:, :D]), "w_out1": tiles(i["nsa_w_out"][0]),
        "mod_b": columns(i["ada_b"][0], i["kv_ada_b"], i["ada_b"][1]),
        "gains": columns(i["norm_mix"][0], i["norm_ffn"][0], i["kv_norm"], i["norm_mix"][1], i["norm_ffn"][1]).reshape(P, 5, DC),
        "small": C(np.concatenate([np.concatenate([i["diff_q_gain"][0]] * 2)[None], np.concatenate([i["diff_k_gain"][0]] * 2)[None],
                                   i["diff_subln"], i["nsa_k_gain"], i["nsa_q_gain"], i["cmp_b1"].reshape(4, P)]).T),
        "lam": C(i["diff_lambda"][0].T),
        "rel": C(i["rel_bias"]),
        "w2": C(i["cmp_w2"].reshape(2, 2, P, P).transpose(2, 0, 1, 3)),
        "pos_t": C(i["cmp_pos"].transpose(2, 0, 1)),
        "w_gate": C(i["nsa_w_in"][0][:, D:].reshape(DC, P, 24).transpose(1, 0, 2)),
        "b_gate": C(i["nsa_b_gate"]),
    }
    for l in range(2):
        arrays[f"w_q{l}"] = tiles(i["peer_w_q"][l])
        arrays[f"subkeys{l}"] = C(i["peer_subkeys"][l].transpose(2, 0, 1))
        arrays[f"u{l}"] = C(i["peer_u"][l].reshape(KEYS, KEYS, DC, P).transpose(1, 3, 2, 0))
        arrays[f"v{l}"] = i["peer_v"][l]

    two = np.kron(np.eye(2), np.ones((64, 64)))
    arrays["const"] = C(np.stack([np.eye(P), np.ones((P, P)), two, np.tile(np.arange(P), (P, 1))], 1).astype(np.float32))
    token = np.arange(T).reshape(TT, P).T[:, :, None]
    arrays["mask_c"] = (token >= CMP_STRIDE * np.arange(N_CMP) + CMP_LEN - 1).astype(np.float32)
    arrays["onehot_dist"] = distance_buckets()

    nc = bacc.Bacc("TRN2", target_bir_lowering=False, num_devices=1)
    arrays = {f"in_{k}": C(v) for k, v in arrays.items()}
    a = {k[3:]: nc.dram_tensor(k, v.shape, F32, kind="ExternalInput").ap() for k, v in arrays.items()}
    for l in range(2):
        a[f"v{l}"] = a[f"v{l}"].rearrange("(i j) (c n) -> j i c n", j=KEYS, n=P)
    a["act_scratch"] = nc.dram_tensor("act_scratch", (KEYS, P, T), F32, kind="Internal").ap()
    a["out"] = nc.dram_tensor("out_t", (P, DC, T), F32, kind="ExternalOutput").ap()
    build(nc, a)
    r = run_bass_kernel_spmd(nc, [arrays], core_ids=[0])
    return C(r.results[0]["out_t"].transpose(1, 0, 2).reshape(D, T).T)[None]
```
